# Optimizing a Trainium2 kernel written in Bass

```python
import math
import jax, jax.numpy as jnp
from jax import lax
import numpy as np

D_MODEL = 1024
BATCH = 1
SEQ = 256
DEPTH = 2

CHUNK = 64
Q_BLOCK = 128
SPARSE_Q_BLOCK = 64
TOKEN_BLOCK = 128

D_MIX = D_MODEL
DIFF_WIDTH = D_MIX // 2
DSA_WIDTH = D_MIX - DIFF_WIDTH
DIFF_HEAD_DIM = 64
DIFF_V_DIM = 2 * DIFF_HEAD_DIM
DIFF_HEADS = DIFF_WIDTH // DIFF_V_DIM
DSA_HEAD_DIM = 64
DSA_HEADS = DSA_WIDTH // DSA_HEAD_DIM
IDX_HEADS = 4
IDX_DIM = 64
IDX_TOPK_MAX = 256

DIFF_QK_COLS = DIFF_HEADS * 2 * DIFF_HEAD_DIM
DIFF_V_COLS = DIFF_HEADS * DIFF_V_DIM
DSA_COLS = DSA_HEADS * DSA_HEAD_DIM
IDX_Q_COLS = IDX_HEADS * IDX_DIM
IN_WIDTHS = (DIFF_QK_COLS, DIFF_QK_COLS, DIFF_V_COLS, DSA_COLS, DSA_COLS, DSA_COLS, IDX_Q_COLS, IDX_DIM, IDX_HEADS)
V_SEGMENTS = (2, 5)
IN_COLS = sum(IN_WIDTHS)

PEER_HEADS = 8
PEER_N_KEYS = 128
PEER_N_EXPERTS = PEER_N_KEYS * PEER_N_KEYS
PEER_QUERY_DIM = 256
PEER_HALF_DIM = PEER_QUERY_DIM // 2
PEER_TOPK = 16

PLE_DIM = 256

LN_EPS = 1e-5
DEEPNORM_ALPHA = (2 * DEPTH) ** 0.25
DEEPNORM_BETA = (8 * DEPTH) ** -0.25
NEG_INF = -1e30

kernel_name = "hybrid_diffattn_dsa_peer_deepnorm"

def layer_norm(x, g, b):
    xf = x.astype(jnp.float32)
    mu = jnp.mean(xf, axis=-1, keepdims=True)
    xc = xf - mu
    var = jnp.mean(xc * xc, axis=-1, keepdims=True)
    y = xc * lax.rsqrt(var + LN_EPS) * g.astype(jnp.float32) + b.astype(jnp.float32)
    return y.astype(x.dtype)

def rms_norm(x, g):
    xf = x.astype(jnp.float32)
    y = xf * lax.rsqrt(jnp.mean(xf * xf, axis=-1, keepdims=True) + LN_EPS)
    return y * g.astype(jnp.float32)

def alibi_slopes(n):
    return 2.0 ** (-8.0 * jnp.arange(1, n + 1, dtype=jnp.float32) / n)

def chunk_end(t):
    return (t // CHUNK + 1) * CHUNK

def diff_attention(q, k, v, lam, slopes):
    B, S, H = q.shape[:3]
    nb = S // Q_BLOCK
    scale = DIFF_HEAD_DIM ** -0.5
    kf = k.astype(jnp.float32)
    vf = v.astype(jnp.float32)
    key_pos = jnp.arange(S)
    q_blocks = jnp.moveaxis(q.reshape(B, nb, Q_BLOCK, H, 2, DIFF_HEAD_DIM), 1, 0)

    def block(args):
        qb, bi = args
        t = bi * Q_BLOCK + jnp.arange(Q_BLOCK)
        visible = key_pos[None, :] < chunk_end(t)[:, None]
        bias = -slopes[:, None, None] * jnp.abs(t[:, None] - key_pos[None, :]).astype(jnp.float32)
        s = jnp.einsum('bqhmd,bkhmd->bmhqk', qb.astype(jnp.float32), kf) * scale + bias
        s = jnp.where(visible, s, NEG_INF)
        a = jax.nn.softmax(s, axis=-1)
        w = a[:, 0] - lam * a[:, 1]
        return jnp.einsum('bhqk,bkhe->bqhe', w, vf)

    out = lax.map(block, (q_blocks, jnp.arange(nb)))
    return jnp.moveaxis(out, 0, 1).reshape(B, S, H, DIFF_V_DIM)

def indexed_sparse_attention(q, k, v, qi, ki, wi, slopes, topk):
    B, S, H, d = q.shape
    nb = S // SPARSE_Q_BLOCK
    scale = DSA_HEAD_DIM ** -0.5
    kf = k.astype(jnp.float32)
    vf = v.astype(jnp.float32)
    kif = ki.astype(jnp.float32)
    key_pos = jnp.arange(S)

    def to_blocks(a):
        return jnp.moveaxis(a.reshape((B, nb, SPARSE_Q_BLOCK) + a.shape[2:]), 1, 0)

    def block(args):
        qb, qib, wib, bi = args
        t = bi * SPARSE_Q_BLOCK + jnp.arange(SPARSE_Q_BLOCK)
        end = chunk_end(t)
        visible = key_pos[None, :] < end[:, None]
        dots = jax.nn.relu(jnp.einsum('bqjd,bsd->bqjs', qib.astype(jnp.float32), kif))
        iscore = jnp.einsum('bqj,bqjs->bqs', wib.astype(jnp.float32), dots)
        iscore = jnp.where(visible[None], iscore, NEG_INF)
        _, sel = lax.top_k(iscore, topk)
        valid = sel < end[None, :, None]
        kg = jax.vmap(lambda kk, ii: kk[ii])(kf, sel)
        vg = jax.vmap(lambda vv, ii: vv[ii])(vf, sel)
        s = jnp.einsum('bqhd,bqkhd->bhqk', qb.astype(jnp.float32), kg) * scale
        dist = jnp.abs(t[None, :, None] - sel).astype(jnp.float32)
        s = s - slopes[None, :, None, None] * dist[:, None]
        s = jnp.where(valid[:, None], s, NEG_INF)
        a = jax.nn.softmax(s, axis=-1)
        return jnp.einsum('bhqk,bqkhd->bqhd', a, vg)

    out = lax.map(block, (to_blocks(q), to_blocks(qi), to_blocks(wi), jnp.arange(nb)))
    return jnp.moveaxis(out, 0, 1).reshape(B, S, H, d)

def token_mixers(h, w_in, w_out, lam_vecs, subln_g, lam_init):
    B, S, _ = h.shape
    proj = h @ w_in
    split_points = np.cumsum(IN_WIDTHS)[:-1].tolist()
    dq, dk, dv, sq, sk, sv, iq, ik, iw = jnp.split(proj, split_points, axis=-1)

    lv = lam_vecs.astype(jnp.float32)
    lam = jnp.exp(jnp.sum(lv[0] * lv[1])) - jnp.exp(jnp.sum(lv[2] * lv[3])) + lam_init
    dq = dq.reshape(B, S, DIFF_HEADS, 2, DIFF_HEAD_DIM)
    dk = dk.reshape(B, S, DIFF_HEADS, 2, DIFF_HEAD_DIM)
    dv = dv.reshape(B, S, DIFF_HEADS, DIFF_V_DIM)
    a_out = diff_attention(dq, dk, dv, lam, alibi_slopes(DIFF_HEADS))
    a_out = rms_norm(a_out, subln_g) * (1.0 - lam_init)

    topk = min(IDX_TOPK_MAX, S // 4)
    sq = sq.reshape(B, S, DSA_HEADS, DSA_HEAD_DIM)
    sk = sk.reshape(B, S, DSA_HEADS, DSA_HEAD_DIM)
    sv = sv.reshape(B, S, DSA_HEADS, DSA_HEAD_DIM)
    iq = iq.reshape(B, S, IDX_HEADS, IDX_DIM) * (IDX_DIM ** -0.5)
    iw = iw * (IDX_HEADS ** -0.5)
    b_out = indexed_sparse_attention(sq, sk, sv, iq, ik, iw, alibi_slopes(DSA_HEADS), topk)

    mixed = jnp.concatenate([a_out.reshape(B, S, DIFF_WIDTH), b_out.reshape(B, S, DSA_WIDTH)], axis=-1)
    return mixed.astype(h.dtype) @ w_out

def peer_ffn(h, w_q, sub_keys, u_tab, v_tab):
    B, S, D = h.shape
    nb = (B * S) // TOKEN_BLOCK
    xb = h.reshape(nb, TOKEN_BLOCK, D)
    skf = sub_keys.astype(jnp.float32)

    def block(xt):
        q = (xt @ w_q).reshape(TOKEN_BLOCK, PEER_HEADS, 2, PEER_HALF_DIM).astype(jnp.float32)
        s = jnp.einsum('thcd,hckd->thck', q, skf)
        s1, i1 = lax.top_k(s[:, :, 0], PEER_TOPK)
        s2, i2 = lax.top_k(s[:, :, 1], PEER_TOPK)
        cand = (s1[..., :, None] + s2[..., None, :]).reshape(TOKEN_BLOCK, PEER_HEADS, PEER_TOPK * PEER_TOPK)
        cidx = (i1[..., :, None] * PEER_N_KEYS + i2[..., None, :]).reshape(TOKEN_BLOCK, PEER_HEADS, PEER_TOPK * PEER_TOPK)
        best, pos = lax.top_k(cand, PEER_TOPK)
        eidx = jnp.take_along_axis(cidx, pos, axis=-1)
        g = jax.nn.softmax(best, axis=-1)
        u = u_tab[eidx]
        act = jax.nn.gelu(jnp.einsum('thkd,td->thk', u, xt).astype(jnp.float32), approximate=False)
        vv = v_tab[eidx]
        return jnp.einsum('thk,thkd->td', (g * act).astype(xt.dtype), vv)

    out = lax.map(block, xb)
    return out.reshape(B, S, D)

def setup_inputs(seed: int = 0) -> dict:
    key = jax.random.key(seed)
    ks = jax.random.split(key, 20)
    f32 = jnp.float32
    x = jax.random.normal(ks[0], (BATCH, SEQ, D_MODEL), f32)
    p = jax.random.normal(ks[1], (DEPTH, BATCH, SEQ, PLE_DIM), f32)
    ln_in_g = 1.0 + 0.02 * jax.random.normal(ks[2], (D_MODEL,), f32)
    ln_in_b = 0.02 * jax.random.normal(ks[3], (D_MODEL,), f32)
    col_scale = jnp.concatenate([
        jnp.full((w,), DEEPNORM_BETA if i in V_SEGMENTS else 1.0, f32) for i, w in enumerate(IN_WIDTHS)])
    w_in = jax.random.normal(ks[4], (DEPTH, D_MODEL, IN_COLS), f32) * (D_MODEL ** -0.5) * col_scale
    w_out = jax.random.normal(ks[5], (DEPTH, D_MIX, D_MODEL), f32) * (D_MIX ** -0.5) * DEEPNORM_BETA
    diff_lambda = 0.1 * jax.random.normal(ks[6], (DEPTH, 4, DIFF_HEAD_DIM), f32)
    diff_subln_g = 1.0 + 0.02 * jax.random.normal(ks[7], (DEPTH, DIFF_V_DIM), f32)
    ln1_g = 1.0 + 0.02 * jax.random.normal(ks[8], (DEPTH, D_MODEL), f32)
    ln1_b = 0.02 * jax.random.normal(ks[9], (DEPTH, D_MODEL), f32)
    peer_wq = jax.random.normal(ks[10], (DEPTH, D_MODEL, PEER_HEADS * PEER_QUERY_DIM), f32) * (D_MODEL ** -0.5)
    peer_subkeys = jax.random.normal(ks[11], (DEPTH, PEER_HEADS, 2, PEER_N_KEYS, PEER_HALF_DIM), f32) * (PEER_HALF_DIM ** -0.5)
    peer_u = jax.random.normal(ks[12], (DEPTH, PEER_N_EXPERTS, D_MODEL), f32) * (D_MODEL ** -0.5)
    peer_v = jax.random.normal(ks[13], (DEPTH, PEER_N_EXPERTS, D_MODEL), f32) * (PEER_HEADS ** -0.5) * DEEPNORM_BETA
    ple_wg = jax.random.normal(ks[14], (DEPTH, D_MODEL, D_MODEL), f32) * (D_MODEL ** -0.5)
    ple_bg = 0.02 * jax.random.normal(ks[15], (DEPTH, D_MODEL), f32)
    ple_wp = jax.random.normal(ks[16], (DEPTH, PLE_DIM, D_MODEL), f32) * (PLE_DIM ** -0.5) * DEEPNORM_BETA
    ln2_g = 1.0 + 0.02 * jax.random.normal(ks[17], (DEPTH, D_MODEL), f32)
    ln2_b = 0.02 * jax.random.normal(ks[18], (DEPTH, D_MODEL), f32)
    return {"x": x, "p": p, "ln_in_g": ln_in_g, "ln_in_b": ln_in_b, "w_in": w_in, "w_out": w_out,
            "diff_lambda": diff_lambda, "diff_subln_g": diff_subln_g, "ln1_g": ln1_g, "ln1_b": ln1_b,
            "peer_wq": peer_wq, "peer_subkeys": peer_subkeys, "peer_u": peer_u, "peer_v": peer_v,
            "ple_wg": ple_wg, "ple_bg": ple_bg, "ple_wp": ple_wp, "ln2_g": ln2_g, "ln2_b": ln2_b}

def reference(x, p, ln_in_g, ln_in_b, w_in, w_out, diff_lambda, diff_subln_g, ln1_g, ln1_b,
              peer_wq, peer_subkeys, peer_u, peer_v, ple_wg, ple_bg, ple_wp, ln2_g, ln2_b):
    h = layer_norm(x, ln_in_g, ln_in_b)
    for i in range(DEPTH):
        lam_init = 0.8 - 0.6 * math.exp(-0.3 * i)
        mix = token_mixers(h, w_in[i], w_out[i], diff_lambda[i], diff_subln_g[i], lam_init)
        h = layer_norm(DEEPNORM_ALPHA * h + mix, ln1_g[i], ln1_b[i])
        r = DEEPNORM_ALPHA * h + peer_ffn(h, peer_wq[i], peer_subkeys[i], peer_u[i], peer_v[i])
        gate = jax.nn.sigmoid((r @ ple_wg[i] + ple_bg[i]).astype(jnp.float32)).astype(r.dtype)
        r = r + gate * (p[i] @ ple_wp[i])
        h = layer_norm(r, ln2_g[i], ln2_b[i])
    return h


_drawn_inputs = setup_inputs


def setup_inputs(seed=0):
    import zlib

    import numpy as np

    out = dict(_drawn_inputs(seed))
    spreads = {}
    factors = {'diff_subln_g': 5.968, 'ple_bg': 25.965}
    for name, (base, spread) in spreads.items():
        noise = np.random.default_rng([zlib.crc32(name.encode()), seed]).standard_normal(out[name].shape)
        drawn = base * np.exp(spread * noise) if base else spread * noise
        out[name] = __import__('jax').numpy.asarray(drawn.astype(out[name].dtype))
    for name, factor in factors.items():
        out[name] = (out[name] * factor).astype(out[name].dtype)
    return out
```

```python
from contextlib import ExitStack

import numpy as np

import concourse.bass as bass
from concourse import mybir

F32 = mybir.dt.float32
U32 = mybir.dt.uint32
ALU = mybir.AluOpType
ACT = mybir.ActivationFunctionType
AX = mybir.AxisListType

D = 1024
T = 128
SEQ = 256
TILES = SEQ // T
DEPTH = 2
KC = D // 128
CHUNK = 64
DH = 64
DIFF_HEADS, DSA_HEADS, IDX_HEADS = 4, 8, 4
DV = 128
TOPK = 64
PH = 8
NKEYS = 128
PK = 16
HALVES = 2 * PH
SLOTS = PH * PK
NEXP = NKEYS * NKEYS
PLE = 256
EPS = 1e-5
ALPHA = (2 * DEPTH) ** 0.25
SCALE = DH ** -0.5
FAR = 3.0e33
TAKEN = -3.0e38
LAM_INIT = [0.8 - 0.6 * float(np.exp(-0.3 * i)) for i in range(DEPTH)]
OWIN = 3396


def slopes(n):
    return [2.0 ** (-8.0 * (i + 1) / n) for i in range(n)]


WRING = 8
QK_BLOCKS = 19
U_IW = QK_BLOCKS
U_V = U_IW + 1
U_WO = U_V + 8
U_WQ = U_WO + 8
U_SK = U_WQ + HALVES
MIX_UNITS = U_SK + 2
CLOSE_UNITS = 8 + 2
MIX_AT = CLOSE_UNITS

BANKS = 6
MIX_USES = ["hT0", "hT1", "dq", "dk", "sq", "sk", "iqk", "iw", "dv", "sv", "ds0", "ds1", "ds2", "ds3",
            "ix0", "ix1", "dpt0", "dpt1", "ss0", "ss1", "ss2", "ss3", "dpv", "spt0", "spt1", "spt2", "spt3",
            "spv", "mT0", "mT1", "mix0", "mix1", "h1T0", "h1T1", "pq0", "pq1", "pq2", "pq3",
            "ps0", "ps1", "ps2", "ps3"]
CLOSE_USES = ["rT0", "rT1", "gate0", "gate1", "ple0", "ple1"]

RING = 8
ROUNDS = SLOTS // RING
PAIR = 2
HALF_PAIRS = RING // PAIR // 2

MIX_LINKS = 222
CLOSE_LINKS = 12
NORM_LINKS = 8
HAND_LINKS = 3


MIX_PLAN = {"queries": 1, "keys": 2, "values": 1, "scores": 1, "maxes": 1, "weights": 1, "choose": 1,
            "chosen": 1, "sparse": 1, "output": 1, "merge": 1, "project": 1, "norm1": 2, "ask": 2,
            "query": 2, "top": 1, "top2": 1, "pairs": 1, "pairs2": 1, "resolve": 1, "combine": 2}
CLOSE_PLAN = {"take": 2, "gate": 2, "blend": 2, "store": 0}


def norm_number(run):
    if run.stage == "close":
        return 9 if isinstance(run.n, int) and run.n == 3 else 2 * run.n + 4
    return 2 * run.n + 1


class Uses:

    def __init__(self, places, mix, close):
        self.mix, self.close = mix, close
        self.per = [[sum(1 for x in stage if x == p) for p in range(places)] for stage in (mix, close)]

    def at(self, stage, i, n_mix, n_close):
        seq = self.mix if stage == "mix" else self.close
        p = seq[i]
        return p, n_mix * self.per[0][p] + n_close * self.per[1][p] + seq[:i].count(p)


BANK_USES = Uses(BANKS, [i % BANKS for i in range(len(MIX_USES))], [i % BANKS for i in range(len(CLOSE_USES))])
UNIT_USES = Uses(WRING, [(MIX_AT + i) % WRING for i in range(MIX_UNITS)], [i % WRING for i in range(CLOSE_UNITS)])


class Run:

    def __init__(self, stage, n, layer, tile, n_mix, n_close):
        self.stage, self.n, self.layer, self.tile, self.n_mix, self.n_close = stage, n, layer, tile, n_mix, n_close

    def bank(self, name):
        names = MIX_USES if self.stage == "mix" else CLOSE_USES
        return BANK_USES.at(self.stage, names.index(name), self.n_mix, self.n_close)

    def unit(self, u):
        return UNIT_USES.at(self.stage, u, self.n_mix, self.n_close)


class Links:

    def __init__(self, eng, sem, start, per_run):
        self.eng, self.sem, self.start, self.per_run, self.k = eng, sem, start, per_run, 0

    def one(self):
        self.k += 1
        return 1

    def now(self, back=0):
        return self.start + self.k - back

    def close(self):
        assert self.k == self.per_run, (self.sem.name, self.k, self.per_run)


def build(nc, t):
    x_d, out_d, uv_d, wmix_d, wclose_d, norms_d, dpar_d, bg_d, pT_d, tilec_d, fixed_d = (
        t[k] for k in ("x", "out", "uv", "wmix", "wclose", "norms", "dpar", "bg", "pT", "tilec", "fixed"))
    ctx = ExitStack()
    with ctx:
        def sb(name, shape, dt=F32):
            return ctx.enter_context(nc.sbuf_tensor(name, shape, dt))

        def sem(name):
            return ctx.enter_context(nc.semaphore(name))

        rows = sb("rows", [128, RING, 2 * D])
        wring = sb("wring", [128, WRING, D])
        dqT, dkT = sb("dqT", [128, 4, T]), sb("dkT", [128, 4, SEQ])
        sqT, skT = sb("sqT", [128, 4, T]), sb("skT", [128, 4, SEQ])
        iqT, ikT = sb("iqT", [128, 2, T]), sb("ikT", [128, SEQ])
        val = sb("val", [128, TILES, D])
        iw = sb("iw", [128, IDX_HEADS])
        h, h1, hx, res, mixed = (sb(n, [128, D]) for n in ("h", "h1", "hx", "res", "mixed"))
        xT = sb("xT", [128, KC, T])
        normp = sb("normp", [128, 2, D])
        sc = sb("sc", [128, 8, SEQ])
        ex = sb("ex", [128, 8, SEQ])
        pT_sb = sb("probsT", [128, 16, T])
        tilec = sb("tilec", [128, 6, SEQ])
        dpar = sb("dpar", [128, 4 * DH + DV])
        bg = sb("bg", [1, D])
        pT = sb("pT", [128, 2, T])
        ident = sb("ident", [128, 128])
        steps16 = sb("steps16", [128, 2, PK])
        zrow, ones = sb("zrow", [1, 512]), sb("ones", [1, 128])
        dg = sb("dg", [128, RING, T])
        far = sb("far", [128, SEQ])
        iscore = sb("iscore", [128, SEQ])
        m8 = sb("m8", [128, 8])
        mx, nmx, den, rden = (sb(n, [128, 8]) for n in ("mx", "nmx", "den", "rden"))
        sden, snmx, smx, srd = (sb(n, [128, 8]) for n in ("sden", "snmx", "smx", "srd"))
        lamw = sb("lamw", [128, 8])
        ssq = sb("ssq", [128, 8])
        stats, mv, rstd = sb("stats", [128, 2, 6]), sb("mv", [128, 2]), sb("rstd", [128, 3])
        v16 = sb("v16", [128, HALVES, PK])
        i16 = sb("i16", [128, HALVES, PK], U32)
        i16f = sb("i16f", [128, HALVES, PK])
        best = sb("best", [128, PH, PK])
        pos = sb("pos", [128, PH, PK], U32)
        posb = sb("posb", [128, 2, SLOTS], U32)
        posf = sb("posf", [128, 2, SLOTS])
        sel = sb("sel", [128, 2, SLOTS])
        gsum = sb("gsum", [128, 2, PH])
        g_next, g_cur = sb("g_next", [128, SLOTS]), sb("g_cur", [128, SLOTS])
        rows_of = sb("rows_of", [128, 2, SLOTS], U32)
        icur = sb("icur", [128, 2, RING], U32)
        dots, gel = sb("dots", [128, RING]), sb("gel", [128, RING])

        acc = ctx.enter_context(nc.psum_tensor("acc", [128, D], F32))
        banks = [ctx.enter_context(nc.psum_tensor(f"bank{i}", [128, 512], F32)) for i in range(BANKS)]

        s_fixed, s_zeroed = sem("fixed_landed"), sem("keys_zeroed")
        unit_landed = [sem(f"unit_landed{i}") for i in range(WRING)]
        unit_used = [sem(f"unit_used{i}") for i in range(WRING)]
        bank_full = [sem(f"bank_full{i}") for i in range(BANKS)]
        bank_taken = [sem(f"bank_taken{i}") for i in range(BANKS)]
        row_landed = [sem(f"row_landed{i}") for i in range(RING)]
        x_landed, norm_landed, norm_done = sem("x_landed"), sem("norm_landed"), sem("norm_done")
        tilec_landed, dpar_landed = sem("tilec_landed"), sem("dpar_landed")
        bg_landed, pT_landed = sem("bg_landed"), sem("pT_landed")
        h_ready, dmax_ready, dexp_ready = sem("h_ready"), sem("dmax_ready"), sem("dexp_ready")
        lamsum_ready, lamexp_ready = sem("lamsum_ready"), sem("lamexp_ready")
        dw_ready = sem("dw_ready")
        smax_ready, sexp_ready = sem("smax_ready"), sem("sexp_ready")
        mixed_ready, h1_ready = sem("mixed_ready"), sem("h1_ready")
        best_ready, gexp_ready, choice_ready = sem("best_ready"), sem("gexp_ready"), sem("choice_ready")
        res_ready = sem("res_ready")
        var_ready, rstd_ready, ms_ready, rms_ready = (sem(n) for n in ("var_ready", "rstd_ready", "ms_ready", "rms_ready"))
        acc_taken, ple_done = sem("acc_taken"), sem("ple_done")
        idx_staged, dot_ready, gelu_ready, diag_ready, slot_done = (
            sem(n) for n in ("idx_staged", "dot_ready", "gelu_ready", "diag_ready", "slot_done"))
        mix_link, close_link, norm_link, hand_link = (sem(n) for n in ("mix_link", "close_link", "norm_link", "hand_link"))
        waits_passed = sem("waits_passed")
        out_stored = sem("out_stored")

        block = ctx.enter_context(nc.Block())

        def alone(eng):
            eng.sem_inc(waits_passed, 1)

        def drive(eng, seg, rounds):
            def stage(name, run, s, plan, at=0):
                for part in MIX_PLAN if name == "mix" else CLOSE_PLAN:
                    seg(name, run, part)
                    if s is not None and plan[part]:
                        rounds(s, at, plan[part])
                        at += plan[part]
                return at

            seg("norm", Run("norm", 0, 0, 0, 0, 0), "embed")
            stage("mix", Run("mix", 0, 0, 0, 0, 0), None, None)
            seg("hand", Run("hand", 0, 0, 0, 1, 0), "over")
            seg("norm", Run("norm", 1, 0, 1, 1, 0), "embed")
            plan = {**MIX_PLAN, "keys": MIX_PLAN["keys"] + sum(CLOSE_PLAN.values())}
            assert stage("mix", Run("mix", 1, 0, 1, 1, 0), 0, plan) == 2 * ROUNDS
            with eng.Fori(0, TILES) as tile:
                seg("hand", Run("hand", tile + 1, 0, tile, tile + 2, tile), "over")
                at = stage("close", Run("close", tile, 0, tile, tile + 2, tile), tile + 1, CLOSE_PLAN)
                at = stage("mix", Run("mix", tile + 2, 1, tile, tile + 2, tile + 1), tile + 1, MIX_PLAN, at)
                assert at == 2 * ROUNDS
            seg("hand", Run("hand", 3, 1, 1, 4, 2), "over")
            stage("close", Run("close", 2, 1, 0, 4, 2), 3, {"take": 1, "gate": 1, "blend": 2 * ROUNDS - 2, "store": 0})
            seg("hand", Run("hand", 4, 1, 1, 4, 3), "over")
            stage("close", Run("close", 3, 1, 1, 4, 3), None, None)

        def looped(eng, half_round):
            def rounds(s, first, count):
                end = first + count
                if first % 2:
                    half_round(s, first // 2, 1)
                    first += 1
                if end - first >= 4:
                    with eng.Fori(first // 2, end // 2) as r:
                        half_round(s, r, 0)
                        half_round(s, r, 1)
                elif end - first >= 2:
                    half_round(s, first // 2, 0)
                    half_round(s, first // 2, 1)
                if end % 2 and end > first:
                    half_round(s, end // 2, 0)
            return rounds

        def taken(run, name):
            b, before = run.bank(name)
            return bank_taken[b], before + 1

        @block.sync
        def _(sp):
            sp.dma_start(ident[:], fixed_d[:, 0:128]).then_inc(s_fixed, 16)
            sp.dma_start(steps16[:].rearrange("p a k -> p (a k)"), fixed_d[:, 128:160]).then_inc(s_fixed, 16)

            def at(array, i):
                return array[i] if isinstance(i, int) else array[bass.ds(i, 1)].rearrange("a p n -> (a p) n")

            def unit(run, table, u):
                slot, before = run.unit(u)
                if not (isinstance(before, int) and before == 0):
                    sp.wait_ge(unit_used[slot], before)
                sp.dma_start(wring[:, slot, :], table[run.layer, u]).then_inc(unit_landed[slot], 16)

            def norm_params(row, q):
                if not (isinstance(q, int) and q == 0):
                    sp.wait_ge(norm_done, q)
                sp.dma_start(normp[:].rearrange("p a d -> p (a d)"),
                             norms_d[row:row + 1, :].broadcast_to([128, 2 * D])).then_inc(norm_landed, 16)

            def seg(stage, run, part):
                if stage == "norm":
                    if run.n:
                        sp.wait_ge(norm_done, 2)
                    sp.dma_start(res[:], at(x_d, run.tile)).then_inc(x_landed, 16)
                    norm_params(0, 2 * run.n)
                if stage == "mix" and part == "queries":
                    for u in range(0, 12):
                        unit(run, wmix_d, u)
                    if not (isinstance(run.n, int) and run.n == 0):
                        sp.wait_ge(choice_ready, run.n)
                    sp.dma_start(tilec[:].rearrange("p a k -> p (a k)"), at(tilec_d, run.tile)).then_inc(tilec_landed, 16)
                    sp.dma_start(dpar[:], dpar_d[run.layer:run.layer + 1, :].broadcast_to([128, 4 * DH + DV])
                                 ).then_inc(dpar_landed, 16)
                    for u in range(12, U_V):
                        unit(run, wmix_d, u)
                if stage == "mix" and part == "values":
                    for u in range(U_V, U_WO):
                        unit(run, wmix_d, u)
                if stage == "mix" and part == "choose":
                    norm_params(1 + run.layer, norm_number(run))
                    for u in range(U_WO, U_WQ):
                        unit(run, wmix_d, u)
                if stage == "mix" and part == "project":
                    for u in range(U_WQ, MIX_UNITS):
                        unit(run, wmix_d, u)
                if stage == "close" and part == "take":
                    sp.wait_ge(ple_done, run.n + 1)
                    sp.dma_start(pT[:].rearrange("p a k -> p (a k)"), at(pT_d[run.layer], run.tile)).then_inc(pT_landed, 16)
                    sp.dma_start(bg[:], bg_d[run.layer:run.layer + 1, :]).then_inc(bg_landed, 16)
                    for u in range(CLOSE_UNITS):
                        unit(run, wclose_d, u)
                    norm_params(1 + DEPTH + run.layer, norm_number(run))
                if stage == "close" and part == "store" and run.layer == DEPTH - 1:
                    sp.wait_ge(norm_done, norm_number(run) + 1)
                    sp.dma_start(at(out_d, run.tile), h[:]).then_inc(out_stored, 16)

            drive(sp, seg, lambda s, first, count: None)
            sp.wait_ge(out_stored, 16 * TILES)

        @block.gpsimd
        def _(pool):
            pool.memset(ones[:], 1.0).then_inc(s_zeroed, 1)
            pool.memset(zrow[:], 0.0).then_inc(s_zeroed, 1)
            pool.memset(dkT[:, :, T:], 0.0).then_inc(s_zeroed, 1)
            pool.memset(skT[:, :, T:], 0.0).then_inc(s_zeroed, 1)
            pool.memset(ikT[:, T:], 0.0).then_inc(s_zeroed, 1)
            pool.memset(val[:, 1, :], 0.0).then_inc(s_zeroed, 1)

            def one_round(s, r, half, free):
                pool.tensor_copy(icur[:, half, :],
                                 rows_of[:, s - 2 * (s // 2) if isinstance(s, int) else 2 - s, bass.ds(r * RING, RING)]
                                 ).then_inc(idx_staged, 1)
                pool.wait_ge(idx_staged, s * ROUNDS + r + 1)
                alone(pool)
                for j in range(RING):
                    if free:
                        pool.wait_ge(slot_done, s * SLOTS + r * RING + j + 1 - RING)
                        alone(pool)
                    pool.indirect_dma_start(
                        out=rows[:, j, :], out_offset=None, in_=uv_d,
                        in_offset=bass.IndirectOffsetOnAxis(ap=icur[:, half, j:j + 1], axis=0),
                    ).then_inc(row_landed[j], 16)

            def step(s, peel):
                pool.wait_ge(choice_ready, s + 1)
                alone(pool)
                if peel:
                    one_round(s, 0, 0, False)
                    one_round(s, 1, 1, True)
                with pool.Fori(1 if peel else 0, ROUNDS // 2) as r2:
                    one_round(s, r2 * 2, 0, True)
                    one_round(s, r2 * 2 + 1, 1, True)

            step(0, True)
            with pool.Fori(0, TILES) as tile:
                step(tile + 1, False)
            step(3, False)

        @block.scalar
        def _(act):
            def take(run, name, out, cols=slice(0, 512), func=ACT.Copy, last=True):
                b, before = run.bank(name)
                act.wait_ge(bank_full[b], before + 1)
                src = banks[b][:, cols]
                if len(out.shape) == 3:
                    src = src.rearrange("p (c t) -> p c t", c=out.shape[1])
                ins = nc.scalar.activation(out, src, func)
                if last:
                    ins.then_inc(bank_taken[b], 1)

            def root(q):
                act.wait_ge(var_ready, q + 1)
                nc.scalar.activation(rstd[:, 2:3], rstd[:, 1:2], ACT.Sqrt).then_inc(rstd_ready, 1)

            def quarter(buf, i):
                return buf[:, 4 * i:4 * i + 4, :].rearrange("p c t -> p (c t)")

            def all_blocks(buf):
                return buf[:].rearrange("p c t -> p (c t)")

            def seg(stage, run, part):
                n, dyn = run.n, not isinstance(run.tile, int)
                cols = bass.ds(run.tile * T, T) if dyn else slice(run.tile * T, run.tile * T + T)
                at_tile = bass.ds(run.tile, 1) if dyn else run.tile
                if stage == "norm":
                    root(2 * n)
                if stage == "close" and part == "blend":
                    root(norm_number(run))
                if stage == "mix" and part == "queries":
                    for i in range(2):
                        take(run, f"hT{i}", quarter(xT, i))
                    if isinstance(n, int) and n == 0:
                        act.wait_ge(s_zeroed, 6)
                    take(run, "dq", all_blocks(dqT))
                    take(run, "dk", dkT[:, :, cols])
                if stage == "mix" and part == "keys":
                    take(run, "sq", all_blocks(sqT))
                    take(run, "sk", skT[:, :, cols])
                    take(run, "iqk", all_blocks(iqT), slice(0, 256), last=False)
                    take(run, "iqk", ikT[:, cols], slice(256, 384))
                if stage == "mix" and part == "values":
                    take(run, "iw", iw[:], slice(0, IDX_HEADS))
                    take(run, "dv", val[:, at_tile, 0:512])
                    take(run, "sv", val[:, at_tile, 512:D])
                if stage == "mix" and part == "scores":
                    for i in range(2):
                        take(run, f"ix{i}", quarter(pT_sb, i), func=ACT.Relu)
                if stage == "mix" and part == "maxes":
                    act.wait_ge(lamsum_ready, n + 1)
                    nc.scalar.activation(lamw[:, 2:4], lamw[:, 0:2], ACT.Exp).then_inc(lamexp_ready, 1)
                    act.wait_ge(dmax_ready, n + 1)
                    for i in range(8):
                        nc.scalar.activation(ex[:, i, :], sc[:, i, :], ACT.Exp, bias=nmx[:, i:i + 1], scale=SCALE,
                                             accum_out=den[:, i:i + 1]).then_inc(dexp_ready, 1)
                if stage == "mix" and part == "choose":
                    for i in range(2):
                        take(run, f"dpt{i}", quarter(pT_sb, i))
                if stage == "mix" and part == "sparse":
                    take(run, "dpv", mixed[:, 0:512])
                    act.wait_ge(smax_ready, n + 1)
                    for i in range(8):
                        nc.scalar.activation(ex[:, i, :], sc[:, i, :], ACT.Exp, bias=snmx[:, i:i + 1], scale=SCALE,
                                             accum_out=sden[:, i:i + 1]).then_inc(sexp_ready, 1)
                if stage == "mix" and part == "output":
                    for i in range(4):
                        take(run, f"spt{i}", quarter(pT_sb, i))
                    act.wait_ge(ms_ready, n + 1)
                    nc.scalar.activation(ssq[:, 4:8], ssq[:, 0:4], ACT.Sqrt).then_inc(rms_ready, 1)
                if stage == "mix" and part == "project":
                    for i in range(2):
                        take(run, f"mT{i}", quarter(xT, i))
                if stage == "mix" and part == "norm1":
                    root(norm_number(run))
                if stage == "mix" and part == "ask":
                    for i in range(2):
                        take(run, f"h1T{i}", quarter(xT, i))
                    for i in range(2):
                        take(run, f"pq{i}", quarter(pT_sb, i))
                if stage == "mix" and part == "query":
                    for i in range(2, 4):
                        take(run, f"pq{i}", quarter(pT_sb, i))
                    for i in range(4):
                        take(run, f"ps{i}", ex[:, 2 * i:2 * i + 2, :].rearrange("p c t -> p (c t)"))
                if stage == "mix" and part == "combine":
                    act.wait_ge(best_ready, n + 1)
                    nc.scalar.activation(g_next[:], g_next[:], ACT.Exp).then_inc(gexp_ready, 1)
                if stage == "close" and part == "gate":
                    for i in range(2):
                        take(run, f"rT{i}", quarter(xT, i))
                    for i in range(2):
                        take(run, f"gate{i}", mixed[:, 512 * i:512 * i + 512], func=ACT.Sigmoid)

            def half_round(s, r, half):
                for i in range(half * HALF_PAIRS, half * HALF_PAIRS + HALF_PAIRS):
                    act.wait_ge(dot_ready, s * SLOTS + r * RING + PAIR * (i + 1))
                    nc.scalar.activation(gel[:, PAIR * i:PAIR * i + PAIR], dots[:, PAIR * i:PAIR * i + PAIR],
                                         ACT.Gelu).then_inc(gelu_ready, 1)

            drive(act, seg, looped(act, half_round))

        @block.vector
        def _(dve):
            V = nc.vector

            def bank(run, name):
                b, before = run.bank(name)
                return banks[b], b, before

            def norm(L, out, q, src=res):
                for i in range(2):
                    V.bn_stats(stats[:, i, :], src[:, 512 * i:512 * i + 512]).then_inc(L.sem, L.one())
                dve.wait_ge(L.sem, L.now())
                alone(dve)
                V.bn_aggr(mv[:], stats[:].rearrange("p a s -> p (a s)")).then_inc(L.sem, L.one())
                dve.wait_ge(L.sem, L.now())
                V.tensor_scalar(rstd[:, 0:1], mv[:, 1:2], EPS, None, ALU.add).then_inc(L.sem, L.one())
                dve.wait_ge(L.sem, L.now())
                V.reciprocal(rstd[:, 1:2], rstd[:, 0:1]).then_inc(L.sem, L.one())
                dve.wait_ge(L.sem, L.now())
                dve.sem_inc(var_ready, 1)
                dve.wait_ge(rstd_ready, q + 1)
                V.tensor_scalar(src[:], src[:], mv[:, 0:1], rstd[:, 2:3], ALU.subtract, ALU.mult).then_inc(L.sem, L.one())
                dve.wait_ge(L.sem, L.now())
                dve.wait_ge(norm_landed, 16 * (q + 1))
                V.tensor_tensor(src[:], src[:], normp[:, 0, :], ALU.mult).then_inc(L.sem, L.one())
                dve.wait_ge(L.sem, L.now())
                return V.tensor_tensor(out[:], src[:], normp[:, 1, :], ALU.add)

            held = {}

            def seg(stage, run, part):
                n = run.n
                name = {"mix": (mix_link, MIX_LINKS), "close": (close_link, CLOSE_LINKS),
                        "norm": (norm_link, NORM_LINKS), "hand": (hand_link, HAND_LINKS)}[stage]
                if held.get("run") is not run:
                    held["run"] = run
                    held["L"] = Links(dve, name[0], n * name[1], name[1])
                L = held["L"]

                if stage == "norm":
                    dve.wait_ge(x_landed, 16 * (n + 1))
                    norm(L, h, 2 * n).then_inc(L.sem, L.one())
                    dve.wait_ge(L.sem, L.now())
                    dve.sem_inc(norm_done, 1)
                    dve.sem_inc(h_ready, 1)
                    L.close()
                if stage == "hand":
                    if not (isinstance(n, int) and n == 0):
                        dve.wait_ge(slot_done, n * SLOTS)
                        V.scalar_tensor_tensor(res[:], hx[:], ALPHA, acc[:], ALU.mult, ALU.add).then_inc(L.sem, L.one())
                        dve.wait_ge(L.sem, L.now())
                        dve.sem_inc(acc_taken, 1)
                        if isinstance(n, int) and n == 4:
                            dve.sem_inc(res_ready, 1)
                            return
                    else:
                        dve.sem_inc(hand_link, 1); L.k += 1
                    dve.wait_ge(h1_ready, n + 1)
                    V.tensor_copy(hx[:], h1[:]).then_inc(L.sem, L.one())
                    V.tensor_copy(g_cur[:], g_next[:]).then_inc(L.sem, L.one())
                    dve.wait_ge(L.sem, L.now())
                    if not (isinstance(n, int) and n == 0):
                        dve.sem_inc(res_ready, 1)
                    L.close()

                if stage == "mix" and part == "maxes":
                    dve.wait_ge(tilec_landed, 16 * (n + 1))
                    dve.wait_ge(dpar_landed, 16 * (n + 1))
                    for i in range(2):
                        V.tensor_tensor_reduce(out=res[:, DH * i:DH * i + DH], in0=dpar[:, 128 * i:128 * i + 64],
                                               in1=dpar[:, 128 * i + 64:128 * i + 128], scale=1.0, scalar=0.0,
                                               op0=ALU.mult, op1=ALU.add, accum_out=lamw[:, i:i + 1]).then_inc(L.sem, L.one())
                    dve.wait_ge(L.sem, L.now())
                    dve.sem_inc(lamsum_ready, 1)
                    for i in range(4):
                        bk, b, before = bank(run, f"ds{i}")
                        dve.wait_ge(bank_full[b], before + 1)
                        alone(dve)
                        for a in range(2):
                            hd, m = 2 * (i // 2) + a, i % 2
                            V.tensor_tensor_reduce(out=sc[:, 2 * hd + m, :], in0=bk[:, SEQ * a:SEQ * a + SEQ],
                                                   in1=tilec[:, hd, :], scale=1.0, scalar=-3.0e38,
                                                   op0=ALU.add, op1=ALU.max, accum_out=mx[:, 2 * hd + m:2 * hd + m + 1]).then_inc(L.sem, L.one())
                        dve.wait_ge(L.sem, L.now())
                        dve.sem_inc(bank_taken[b], 1)
                    V.tensor_scalar(nmx[:], mx[:], -SCALE, None, ALU.mult).then_inc(L.sem, L.one())
                    dve.wait_ge(L.sem, L.now())
                    dve.sem_inc(dmax_ready, 1)
                    relu = pT_sb[:, 0:8, :].rearrange("p (j a) t -> p j (a t)", a=2)
                    for i in range(IDX_HEADS):
                        if i % 2 == 0:
                            dve.wait_ge(*taken(run, f"ix{i // 2}"))
                        j = i // 2 + 2 * (i % 2)
                        V.scalar_tensor_tensor(iscore[:], relu[:, i, :], iw[:, j:j + 1],
                                               tilec[:, 5, :] if i == 0 else iscore[:], ALU.mult, ALU.add).then_inc(L.sem, L.one())
                        dve.wait_ge(L.sem, L.now())
                if stage == "mix" and part == "weights":
                    dve.wait_ge(lamexp_ready, n + 1)
                    V.tensor_tensor(lamw[:, 4:5], lamw[:, 3:4], lamw[:, 2:3], ALU.subtract).then_inc(L.sem, L.one())
                    dve.wait_ge(L.sem, L.now())
                    V.tensor_scalar(lamw[:, 5:6], lamw[:, 4:5], -LAM_INIT[run.layer], None, ALU.add).then_inc(L.sem, L.one())
                    dve.wait_ge(dexp_ready, 8 * (n + 1))
                    V.reciprocal(rden[:], den[:]).then_inc(L.sem, L.one())
                    dve.wait_ge(L.sem, L.now())
                    V.tensor_scalar(nmx[:], rden[:], lamw[:, 5:6], None, ALU.mult).then_inc(L.sem, L.one())
                    dve.wait_ge(L.sem, L.now())
                    for hd in range(DIFF_HEADS):
                        V.tensor_scalar(ex[:, 2 * hd + 1, :], ex[:, 2 * hd + 1, :], nmx[:, 2 * hd + 1:2 * hd + 2],
                                        None, ALU.mult).then_inc(L.sem, L.one())
                    for hd in range(DIFF_HEADS):
                        dve.wait_ge(L.sem, L.now(DIFF_HEADS - 1))
                        V.scalar_tensor_tensor(sc[:, hd, :], ex[:, 2 * hd, :], rden[:, 2 * hd:2 * hd + 1],
                                               ex[:, 2 * hd + 1, :], ALU.mult, ALU.add).then_inc(L.sem, L.one())
                    dve.wait_ge(L.sem, L.now())
                    dve.sem_inc(dw_ready, 1)
                if stage == "mix" and part == "choose":
                    for i in range(TOPK // 16):
                        alone(dve)
                        V.max(m8[:], iscore[:]).then_inc(L.sem, L.one())
                        dve.wait_ge(L.sem, L.now())
                        alone(dve)
                        V.match_replace(iscore[:], m8[:], iscore[:], TAKEN).then_inc(L.sem, L.one())
                        dve.wait_ge(L.sem, L.now())
                if stage == "mix" and part == "chosen":
                    for i in range(TOPK // 16):
                        alone(dve)
                        V.max(m8[:], iscore[:]).then_inc(L.sem, L.one())
                        dve.wait_ge(L.sem, L.now())
                        alone(dve)
                        V.match_replace(iscore[:], m8[:], iscore[:], TAKEN).then_inc(L.sem, L.one())
                        dve.wait_ge(L.sem, L.now())
                    V.tensor_scalar(far[:], iscore[:], TAKEN, FAR, ALU.not_equal, ALU.mult).then_inc(L.sem, L.one())
                    dve.wait_ge(L.sem, L.now())
                    V.tensor_tensor(far[:], far[:], tilec[:, 4, :], ALU.add).then_inc(L.sem, L.one())
                    dve.wait_ge(L.sem, L.now())
                if stage == "mix" and part == "sparse":
                    slope = slopes(DSA_HEADS)
                    dve.wait_ge(*taken(run, "dpt1"))
                    for i in range(4):
                        bk, b, before = bank(run, f"ss{i}")
                        dve.wait_ge(bank_full[b], before + 1)
                        for a in range(2):
                            hd = 4 * (i // 2) + 2 * a + i % 2
                            V.scalar_tensor_tensor(sc[:, hd, :], far[:], -slope[hd] / SCALE,
                                                   bk[:, SEQ * a:SEQ * a + SEQ], ALU.mult, ALU.add).then_inc(L.sem, L.one())
                        dve.wait_ge(L.sem, L.now())
                        dve.sem_inc(bank_taken[b], 1)
                    V.tensor_reduce(smx[:], sc[:], axis=AX.X, op=ALU.max).then_inc(L.sem, L.one())
                    dve.wait_ge(L.sem, L.now())
                    V.tensor_scalar(snmx[:], smx[:], -SCALE, None, ALU.mult).then_inc(L.sem, L.one())
                    dve.wait_ge(L.sem, L.now())
                    dve.sem_inc(smax_ready, 1)
                if stage == "mix" and part == "output":
                    dve.wait_ge(*taken(run, "dpv"))
                    for hd in range(DIFF_HEADS):
                        cols = mixed[:, DV * hd:DV * hd + DV]
                        V.tensor_tensor_reduce(out=res[:, DV * hd:DV * hd + DV], in0=cols, in1=cols, scale=1.0, scalar=0.0,
                                               op0=ALU.mult, op1=ALU.add, accum_out=ssq[:, hd:hd + 1]).then_inc(L.sem, L.one())
                    dve.wait_ge(L.sem, L.now())
                    V.tensor_scalar(ssq[:, 4:8], ssq[:, 0:4], 1.0 / DV, EPS, ALU.mult, ALU.add).then_inc(L.sem, L.one())
                    dve.wait_ge(L.sem, L.now())
                    V.reciprocal(ssq[:, 0:4], ssq[:, 4:8]).then_inc(L.sem, L.one())
                    dve.wait_ge(L.sem, L.now())
                    dve.sem_inc(ms_ready, 1)
                    dve.wait_ge(rms_ready, n + 1)
                    V.tensor_scalar(ssq[:, 0:4], ssq[:, 4:8], 1.0 - LAM_INIT[run.layer], None, ALU.mult).then_inc(L.sem, L.one())
                    dve.wait_ge(L.sem, L.now())
                    for hd in range(DIFF_HEADS):
                        cols = mixed[:, DV * hd:DV * hd + DV]
                        V.scalar_tensor_tensor(cols, cols, ssq[:, hd:hd + 1], dpar[:, 4 * DH:], ALU.mult, ALU.mult).then_inc(L.sem, L.one())
                if stage == "mix" and part == "merge":
                    dve.wait_ge(sexp_ready, 8 * (n + 1))
                    V.reciprocal(srd[:], sden[:]).then_inc(L.sem, L.one())
                    dve.wait_ge(L.sem, L.now())
                    bk, b, before = bank(run, "spv")
                    dve.wait_ge(bank_full[b], before + 1)
                    V.tensor_tensor(mixed[:, 512:D].rearrange("p (h e) -> p h e", e=DH),
                                    bk[:].rearrange("p (h e) -> p h e", e=DH),
                                    srd[:, :, None].broadcast_to([128, 8, DH]), ALU.mult).then_inc(L.sem, L.one())
                    dve.wait_ge(L.sem, L.now())
                    dve.sem_inc(bank_taken[b], 1)
                    dve.sem_inc(mixed_ready, 1)
                if stage == "mix" and part == "norm1":
                    for i in range(2):
                        bk, b, before = bank(run, f"mix{i}")
                        dve.wait_ge(bank_full[b], before + 1)
                        V.scalar_tensor_tensor(res[:, 512 * i:512 * i + 512], h[:, 512 * i:512 * i + 512], ALPHA,
                                               bk[:], ALU.mult, ALU.add).then_inc(L.sem, L.one())
                        dve.wait_ge(L.sem, L.now())
                        dve.sem_inc(bank_taken[b], 1)
                    norm(L, h1, norm_number(run)).then_inc(L.sem, L.one())
                    dve.wait_ge(L.sem, L.now())
                    dve.sem_inc(norm_done, 1)
                    dve.sem_inc(h1_ready, 1)

                def top16(lists):
                    alone(dve)
                    for src, vals, idx in lists:
                        V.max(vals[:, 0:8], src).then_inc(L.sem, L.one())
                    dve.wait_ge(L.sem, L.now())
                    alone(dve)
                    for src, vals, idx in lists:
                        V.max_index(idx[:, 0:8], vals[:, 0:8], src).then_inc(L.sem, L.one())
                    dve.wait_ge(L.sem, L.now())
                    alone(dve)
                    for src, vals, idx in lists:
                        V.match_replace(src, vals[:, 0:8], src, TAKEN).then_inc(L.sem, L.one())
                    dve.wait_ge(L.sem, L.now())
                    alone(dve)
                    for src, vals, idx in lists:
                        V.max(vals[:, 8:16], src).then_inc(L.sem, L.one())
                    dve.wait_ge(L.sem, L.now())
                    alone(dve)
                    for src, vals, idx in lists:
                        V.max_index(idx[:, 8:16], vals[:, 8:16], src).then_inc(L.sem, L.one())
                    dve.wait_ge(L.sem, L.now())

                keys = ex[:].rearrange("p a k -> p (a k)").rearrange("p (c k) -> p c k", k=NKEYS)
                cand = sc[:].rearrange("p h (a b) -> p h a b", a=PK)
                if stage == "mix" and part == "top":
                    dve.wait_ge(*taken(run, "ps1"))
                    top16([(keys[:, c, :], v16[:, c, :], i16[:, c, :]) for c in range(0, HALVES // 2)])
                if stage == "mix" and part == "top2":
                    dve.wait_ge(*taken(run, "ps3"))
                    top16([(keys[:, c, :], v16[:, c, :], i16[:, c, :]) for c in range(HALVES // 2, HALVES)])
                    V.tensor_copy(i16f[:], i16[:]).then_inc(L.sem, L.one())
                    for hd in range(PH):
                        V.tensor_tensor(cand[:, hd], v16[:, 2 * hd, :, None].broadcast_to([128, PK, PK]),
                                        v16[:, 2 * hd + 1, None, :].broadcast_to([128, PK, PK]),
                                        ALU.add).then_inc(L.sem, L.one())
                    dve.wait_ge(L.sem, L.now())
                if stage == "mix" and part == "pairs":
                    top16([(sc[:, hd, :], best[:, hd, :], pos[:, hd, :]) for hd in range(PH // 2)])
                if stage == "mix" and part == "pairs2":
                    top16([(sc[:, hd, :], best[:, hd, :], pos[:, hd, :]) for hd in range(PH // 2, PH)])
                g3 = g_next[:].rearrange("p (h k) -> p h k", k=PK)
                lists = i16f[:].rearrange("p (h c) k -> p h c k", c=2)
                hot = ex[:].rearrange("p a k -> p (a k)").rearrange("p (s j) -> p s j", j=PK)
                hot4 = ex[:].rearrange("p a k -> p (a k)").rearrange("p (h s j) -> p h s j", s=PK, j=PK)

                def resolve(c):
                    V.tensor_tensor(hot, posf[:, c, :, None].broadcast_to([128, SLOTS, PK]),
                                    steps16[:, 1 - c, None, :].broadcast_to([128, SLOTS, PK]), ALU.is_equal).then_inc(L.sem, L.one())
                    dve.wait_ge(L.sem, L.now())
                    V.tensor_tensor(hot4, hot4, lists[:, :, c, None, :].broadcast_to([128, PH, PK, PK]), ALU.mult).then_inc(L.sem, L.one())
                    dve.wait_ge(L.sem, L.now())
                    V.tensor_reduce(sel[:, c, :], hot, axis=AX.X, op=ALU.add).then_inc(L.sem, L.one())
                    dve.wait_ge(L.sem, L.now())
                if stage == "mix" and part == "resolve":
                    if not (isinstance(n, int) and n == 0):
                        dve.wait_ge(hand_link, HAND_LINKS * n)
                    V.tensor_tensor(g3, best[:], best[:, :, 0:1].broadcast_to([128, PH, PK]), ALU.subtract).then_inc(L.sem, L.one())
                    dve.wait_ge(L.sem, L.now())
                    dve.sem_inc(best_ready, 1)
                    p_all = pos[:].rearrange("p h k -> p (h k)")
                    V.tensor_scalar(posb[:, 0, :], p_all, 240, None, ALU.bitwise_and).then_inc(L.sem, L.one())
                    V.tensor_scalar(posb[:, 1, :], p_all, 15, None, ALU.bitwise_and).then_inc(L.sem, L.one())
                    dve.wait_ge(L.sem, L.now())
                    V.tensor_copy(posf[:], posb[:]).then_inc(L.sem, L.one())
                    dve.wait_ge(L.sem, L.now())
                    resolve(0)
                if stage == "mix" and part == "combine":
                    resolve(1)
                    V.scalar_tensor_tensor(sel[:, 0, :], sel[:, 0, :], float(NKEYS), sel[:, 1, :], ALU.mult, ALU.add).then_inc(L.sem, L.one())
                    dve.wait_ge(L.sem, L.now())
                    par = n - 2 * (n // 2) if isinstance(n, int) else run.tile
                    V.tensor_scalar(rows_of[:, par, :] if isinstance(par, int) else rows_of[:, bass.ds(par, 1), :],
                                    sel[:, 0, :], float(run.layer * NEXP), None, ALU.add).then_inc(L.sem, L.one())
                    dve.wait_ge(gexp_ready, n + 1)
                    V.tensor_reduce(gsum[:, 0, :], g3, axis=AX.X, op=ALU.add).then_inc(L.sem, L.one())
                    dve.wait_ge(L.sem, L.now())
                    V.reciprocal(gsum[:, 1, :], gsum[:, 0, :]).then_inc(L.sem, L.one())
                    dve.wait_ge(L.sem, L.now())
                    V.tensor_tensor(g3, g3, gsum[:, 1, :, None].broadcast_to([128, PH, PK]), ALU.mult).then_inc(L.sem, L.one())
                    dve.wait_ge(L.sem, L.now())
                    dve.sem_inc(choice_ready, 1)
                    L.close()
                if stage == "close" and part == "blend":
                    dve.wait_ge(*taken(run, "gate1"))
                    for i in range(2):
                        bk, b, before = bank(run, f"ple{i}")
                        dve.wait_ge(bank_full[b], before + 1)
                        cols = slice(512 * i, 512 * i + 512)
                        V.tensor_tensor(mixed[:, cols], mixed[:, cols], bk[:], ALU.mult).then_inc(L.sem, L.one())
                        dve.wait_ge(L.sem, L.now())
                        dve.sem_inc(bank_taken[b], 1)
                    V.tensor_tensor(res[:], res[:], mixed[:], ALU.add).then_inc(L.sem, L.one())
                    dve.wait_ge(L.sem, L.now())
                    if run.layer == DEPTH - 1 and n == 3:
                        dve.wait_ge(out_stored, 16)
                    norm(L, h, norm_number(run)).then_inc(L.sem, L.one())
                    dve.wait_ge(L.sem, L.now())
                    dve.sem_inc(norm_done, 1)
                    if run.layer == 0:
                        dve.sem_inc(h_ready, 1)
                    dve.sem_inc(close_link, CLOSE_LINKS - L.k)
                    L.k = CLOSE_LINKS
                    L.close()

            def half_round(s, r, half):
                def dot(j):
                    dve.wait_ge(row_landed[j], 16 * (s * ROUNDS + r + 1))
                    V.tensor_tensor_reduce(out=rows[:, j, 0:D], in0=rows[:, j, 0:D], in1=hx[:], scale=1.0, scalar=0.0,
                                           op0=ALU.mult, op1=ALU.add, accum_out=dots[:, j:j + 1]).then_inc(dot_ready, 1)

                def diag(i):
                    dve.wait_ge(gelu_ready, s * (SLOTS // PAIR) + r * (RING // PAIR) + i + 1)
                    for j in range(PAIR * i, PAIR * i + PAIR):
                        V.tensor_scalar(dg[:, j, :], ident[:], gel[:, j:j + 1], g_cur[:, bass.ds(r * RING + j, 1)],
                                        ALU.mult, ALU.mult).then_inc(diag_ready, 1)

                pairs = range(half * HALF_PAIRS, half * HALF_PAIRS + HALF_PAIRS)
                for i in pairs:
                    for j in range(PAIR * i, PAIR * i + PAIR):
                        dot(j)
                    if i > pairs[0]:
                        diag(i - 1)
                diag(pairs[-1])

            dve.wait_ge(s_fixed, 32)
            drive(dve, seg, looped(dve, half_round))

        @block.tensor
        def _(pe):
            MM = nc.tensor.matmul

            def bank(run, name):
                b, before = run.bank(name)
                if not (isinstance(before, int) and before == 0):
                    pe.wait_ge(bank_taken[b], before)
                return banks[b], bank_full[b]

            def unit(run, u):
                slot, before = run.unit(u)
                pe.wait_ge(unit_landed[slot], 16 * (before + 1))
                return wring[:, slot, :], unit_used[slot]

            def transposes(run, names, src):
                for i, name in enumerate(names):
                    bk, full = bank(run, name)
                    for k in range(4):
                        ins = nc.tensor.transpose(bk[:, T * k:T * k + T], src(4 * i + k), ident[:])
                    ins.then_inc(full, 1)

            def fill(run, name, ins, used=()):
                b, before = run.bank(name)
                ins.then_inc(bank_full[b], 1)
                pe.wait_ge(bank_full[b], before + 1)
                for s in used:
                    pe.sem_inc(s, 1)

            def by_tokens(run, name, u, bias=None):
                bk, _ = bank(run, name)
                for q in range(4):
                    w, used = unit(run, u + q)
                    for c in range(2):
                        ins = MM(bk[:], xT[:, 2 * q + c, :], w[:, 512 * c:512 * c + 512], start=(q == 0 and c == 0),
                                 stop=(q == 3 and c == 1 and bias is None))
                    if q < 3:
                        ins.then_inc(used, 1)
                if bias is not None:
                    ins = MM(bk[:], ones[:], bias, start=False, stop=True)
                fill(run, name, ins, [used])

            def seg(stage, run, part):
                n = run.n
                if stage == "mix" and part == "queries":
                    pe.wait_ge(h_ready, n + 1)
                    transposes(run, ["hT0", "hT1"], lambda c: h[:, T * c:T * c + T])
                    pe.wait_ge(*taken(run, "hT1"))
                if stage == "mix" and part in ("queries", "keys"):
                    names = ("dq", "dk", "sq", "sk", "iqk")
                    for g in range(0, 2) if part == "queries" else range(2, 5):
                        name = names[g]
                        bk, full = bank(run, name)
                        blocks = range(4 * g, min(4 * g + 4, QK_BLOCKS))
                        for k in blocks:
                            w, used = unit(run, k)
                            for c in range(KC):
                                ins = MM(bk[:, T * (k - 4 * g):T * (k - 4 * g) + T], w[:, T * c:T * c + T], xT[:, c, :],
                                         start=(c == 0), stop=(c == KC - 1))
                            if k < blocks[-1]:
                                ins.then_inc(used, 1)
                        fill(run, name, ins, [used])
                if stage == "mix" and part == "values":
                    bk, full = bank(run, "iw")
                    w, used = unit(run, U_IW)
                    for c in range(KC):
                        ins = MM(bk[:, 0:IDX_HEADS], xT[:, c, :], w[:, T * c:T * c + IDX_HEADS], start=(c == 0), stop=(c == KC - 1))
                    fill(run, "iw", ins, [used])
                    for i, name in enumerate(("dv", "sv")):
                        by_tokens(run, name, U_V + 4 * i)
                if stage == "mix" and part == "scores":
                    pe.wait_ge(*taken(run, "sv"))
                    for i in range(4):
                        bk, full = bank(run, f"ds{i}")
                        rows64 = slice(DH * (i % 2), DH * (i % 2) + DH)
                        for a in range(2):
                            hd = 2 * (i // 2) + a
                            ins = MM(bk[:, SEQ * a:SEQ * a + SEQ], dqT[rows64, hd, :], dkT[rows64, hd, :], start=True, stop=True)
                        ins.then_inc(full, 1)
                    for i in range(2):
                        bk, full = bank(run, f"ix{i}")
                        rows64 = slice(DH * i, DH * i + DH)
                        for a in range(2):
                            ins = MM(bk[:, SEQ * a:SEQ * a + SEQ], iqT[rows64, a, :], ikT[rows64, :], start=True, stop=True)
                        ins.then_inc(full, 1)
                if stage == "mix" and part == "choose":
                    pe.wait_ge(dw_ready, n + 1)
                    transposes(run, ["dpt0", "dpt1"], lambda i: sc[:, i // 2, T * (i % 2):T * (i % 2) + T])
                    for i in range(4):
                        bk, full = bank(run, f"ss{i}")
                        rows64 = slice(DH * (i % 2), DH * (i % 2) + DH)
                        for a in range(2):
                            blk = 2 * (i // 2) + a
                            ins = MM(bk[:, SEQ * a:SEQ * a + SEQ], sqT[rows64, blk, :], skT[rows64, blk, :], start=True, stop=True)
                        ins.then_inc(full, 1)
                if stage == "mix" and part == "sparse":
                    pe.wait_ge(*taken(run, "dpt1"))
                    bk, full = bank(run, "dpv")
                    for hd in range(DIFF_HEADS):
                        for k in range(TILES):
                            ins = MM(bk[:, DV * hd:DV * hd + DV], pT_sb[:, 2 * hd + k, :], val[:, k, DV * hd:DV * hd + DV],
                                     start=(k == 0), stop=(k == TILES - 1))
                    ins.then_inc(full, 1)
                if stage == "mix" and part == "output":
                    pe.wait_ge(sexp_ready, 8 * (n + 1))
                    transposes(run, [f"spt{i}" for i in range(4)], lambda i: ex[:, i // 2, T * (i % 2):T * (i % 2) + T])
                    pe.wait_ge(*taken(run, "spt3"))
                    bk, full = bank(run, "spv")
                    for hd in range(DSA_HEADS):
                        for k in range(TILES):
                            ins = MM(bk[:, DH * hd:DH * hd + DH], pT_sb[:, 2 * hd + k, :],
                                     val[:, k, 512 + DH * hd:512 + DH * hd + DH], start=(k == 0), stop=(k == TILES - 1))
                    ins.then_inc(full, 1)
                if stage == "mix" and part == "project":
                    pe.wait_ge(mixed_ready, n + 1)
                    transposes(run, ["mT0", "mT1"], lambda c: mixed[:, T * c:T * c + T])
                    pe.wait_ge(*taken(run, "mT1"))
                    for i in range(2):
                        by_tokens(run, f"mix{i}", U_WO + 4 * i)
                if stage == "mix" and part == "ask":
                    pe.wait_ge(h1_ready, n + 1)
                    transposes(run, ["h1T0", "h1T1"], lambda c: h1[:, T * c:T * c + T])
                    pe.wait_ge(*taken(run, "h1T1"))
                if stage == "mix" and part in ("ask", "query"):
                    for g in range(0, 2) if part == "ask" else range(2, 4):
                        bk, full = bank(run, f"pq{g}")
                        for k in range(4):
                            w, used = unit(run, U_WQ + 4 * g + k)
                            for c in range(KC):
                                ins = MM(bk[:, T * k:T * k + T], w[:, T * c:T * c + T], xT[:, c, :], start=(c == 0), stop=(c == KC - 1))
                            if k < 3:
                                ins.then_inc(used, 1)
                        fill(run, f"pq{g}", ins, [used])
                if stage == "mix" and part == "query":
                    for g in range(4):
                        pe.wait_ge(*taken(run, f"pq{g}"))
                        bk, full = bank(run, f"ps{g}")
                        if g % 2 == 0:
                            w, used = unit(run, U_SK + g // 2)
                        for k in range(4):
                            at = 4 * (g % 2) + k
                            ins = MM(bk[:, T * k:T * k + T], pT_sb[:, 4 * g + k, :], w[:, T * at:T * at + T], start=True, stop=True)
                        fill(run, f"ps{g}", ins, [used] if g % 2 else [])
                if stage == "hand":
                    if not (isinstance(n, int) and n == 0):
                        pe.wait_ge(acc_taken, n)
                    if not (isinstance(n, int) and n == 4):
                        for i in range(2):
                            MM(acc[:, 512 * i:512 * i + 512], zrow[:, 0:128], zrow[:], start=True, stop=False,
                               skip_group_check=True)
                if stage == "close" and part == "gate":
                    pe.wait_ge(res_ready, n + 1)
                    transposes(run, ["rT0", "rT1"], lambda c: res[:, T * c:T * c + T])
                    pe.wait_ge(*taken(run, "rT1"))
                    pe.wait_ge(bg_landed, 16 * (n + 1))
                    for i in range(2):
                        by_tokens(run, f"gate{i}", 4 * i, bias=bg[:, 512 * i:512 * i + 512])
                    pe.wait_ge(pT_landed, 16 * (n + 1))
                    for i in range(2):
                        bk, full = bank(run, f"ple{i}")
                        w, used = unit(run, 8 + i)
                        for c in range(2):
                            ins = MM(bk[:], pT[:, c, :], w[:, 512 * c:512 * c + 512], start=(c == 0), stop=(c == 1))
                        fill(run, f"ple{i}", ins, [used] + [ple_done] * i)

            def half_round(s, r, half):
                for j in range(half * RING // 2, (half + 1) * RING // 2):
                    pe.wait_ge(diag_ready, s * SLOTS + r * RING + j + 1)
                    for i in range(2):
                        ins = MM(acc[:, 512 * i:512 * i + 512], dg[:, j, :], rows[:, j, D + 512 * i:D + 512 * i + 512],
                                 start=False, stop=False, skip_group_check=True)
                    ins.then_inc(slot_done, 1)

            pe.sem_inc(ple_done, 1)
            pe.wait_ge(s_fixed, 32)
            pe.wait_ge(s_zeroed, 6)
            drive(pe, seg, looped(pe, half_round))


def kernel(x, p, ln_in_g, ln_in_b, w_in, w_out, diff_lambda, diff_subln_g, ln1_g, ln1_b, peer_wq, peer_subkeys,
           peer_u, peer_v, ple_wg, ple_bg, ple_wp, ln2_g, ln2_b):
    import concourse.bacc as bacc
    from concourse.bass_utils import run_bass_kernel_spmd

    def a(v):
        return np.asarray(v)

    def column_block(w):
        return w.reshape(KC, 128, 128).transpose(1, 0, 2).reshape(128, D)

    def halves(w):
        k = w.shape[0] // 256
        return [w[256 * q:256 * q + 256, 512 * i:512 * i + 512].reshape(2, 128, 512).transpose(1, 0, 2).reshape(128, D)
                for i in range(w.shape[1] // 512) for q in range(k)]

    w_in, w_out, peer_wq, peer_subkeys = a(w_in), a(w_out), a(peer_wq), a(peer_subkeys)
    ple_wg, ple_wp = a(ple_wg), a(ple_wp)
    wmix, wclose = [], []
    for i in range(DEPTH):
        w = w_in[i]
        dq, dk, dv, sq, sk, sv = (w[:, 512 * j:512 * j + 512] for j in range(6))
        iq, ik, iwc = w[:, 3072:3328], w[:, 3328:3392], w[:, 3392:OWIN]
        cols = np.concatenate([dq, dk, sq, sk, iq, ik, ik, iwc, np.zeros((D, 128 - IDX_HEADS), w.dtype)], axis=1)
        units = [column_block(cols[:, 128 * b:128 * b + 128]) for b in range(QK_BLOCKS + 1)]
        units += halves(dv) + halves(sv) + halves(w_out[i])
        units += [column_block(peer_wq[i][:, 128 * b:128 * b + 128]) for b in range(HALVES)]
        keys = peer_subkeys[i].reshape(HALVES, NKEYS, 128)
        units += [keys[8 * g:8 * g + 8].transpose(2, 0, 1).reshape(128, D) for g in range(2)]
        wmix.append(np.stack(units))
        wclose.append(np.stack(halves(ple_wg[i]) + halves(ple_wp[i])))
    uv = np.concatenate([a(peer_u), a(peer_v)], axis=2).reshape(DEPTH * NEXP, 2 * D)
    norms = np.concatenate([
        np.stack([a(ln_in_g), *a(ln1_g), *a(ln2_g)]), np.stack([a(ln_in_b), *a(ln1_b), *a(ln2_b)])], axis=1)
    dpar = np.concatenate([a(diff_lambda).reshape(DEPTH, 4 * DH), a(diff_subln_g)], axis=1)
    pT = a(p).reshape(DEPTH, TILES, T, 2, 128).transpose(0, 1, 4, 3, 2).reshape(DEPTH, TILES, 128, 2 * T)

    pos_q, pos_k = np.arange(SEQ)[:, None], np.arange(SEQ)[None, :]
    dist = np.abs(pos_q - pos_k).astype(np.float64)
    seen = pos_k < (pos_q // CHUNK + 1) * CHUNK
    tilec = [np.where(seen, -s * dist / SCALE, -FAR) for s in slopes(DIFF_HEADS)] + [dist, np.where(seen, 0.0, -1e30)]
    tilec = np.stack(tilec, axis=1).astype(np.float32).reshape(TILES, T, 6 * SEQ)
    fixed = np.concatenate([np.eye(128), np.tile(np.arange(PK), (128, 1)), np.tile(PK * np.arange(PK), (128, 1))],
                           axis=1).astype(np.float32)

    arrays = {"x": a(x).reshape(TILES, T, D), "uv": uv, "wmix": np.stack(wmix), "wclose": np.stack(wclose),
              "norms": norms, "dpar": dpar, "bg": a(ple_bg), "pT": pT, "tilec": tilec, "fixed": fixed}
    arrays = {k: np.ascontiguousarray(v) for k, v in arrays.items()}
    nc = bacc.Bacc("TRN2", target_bir_lowering=False, num_devices=1)
    t = {k: nc.dram_tensor(k + "_dram", v.shape, F32, kind="ExternalInput").ap() for k, v in arrays.items()}
    t["out"] = nc.dram_tensor("out_dram", (TILES, T, D), F32, kind="ExternalOutput").ap()
    build(nc, t)
    r = run_bass_kernel_spmd(nc, [{k + "_dram": v for k, v in arrays.items()}], core_ids=[0])
    return r.results[0]["out_dram"].reshape(1, SEQ, D)
```
